# Optimizing a Trainium2 kernel written in Bass

```python
import jax, jax.numpy as jnp
from jax import lax
import numpy as np

D_MODEL = 1024
BATCH = 1
SEQ = 1024
DEPTH = 2
DEC_BATCH = 8
DEC_SEQ = 4
PAST_LEN = 256
PAGE_SIZE = 128

N_A_LAYERS = DEPTH // 2
N_B_LAYERS = DEPTH - N_A_LAYERS
D_RNN = D_MODEL
N_LRU_BLOCKS = 8
LRU_BLOCK = D_RNN // N_LRU_BLOCKS
LRU_C = 8.0
CONV_A_WIDTH = 4
N_HEADS = 16
HEAD_DIM = D_MODEL // N_HEADS
D_FF = 3 * D_MODEL
CONV_F_WIDTH = 3
Q_BLOCK = 128
FORGET_BIAS_OFFSET = 3.0
RMS_EPS = 1e-6

kernel_name = "yoco_hawk_fox_convffn_step"

def rmsnorm(x, g):
    xf = x.astype(jnp.float32)
    y = xf * lax.rsqrt(jnp.mean(xf * xf, axis=-1, keepdims=True) + RMS_EPS)
    return (y * g.astype(jnp.float32)).astype(x.dtype)

def causal_dwconv(x, prev, w, b):
    width = w.shape[0]
    t = x.shape[1]
    xp = jnp.concatenate([prev.astype(x.dtype), x], axis=1)
    y = xp[:, 0:t] * w[0]
    for j in range(1, width):
        y = y + xp[:, j:j + t] * w[j]
    return y + b, xp[:, xp.shape[1] - (width - 1):]

def _lin_combine(c1, c2):
    a1, b1 = c1
    a2, b2 = c2
    return a1 * a2, a2 * b1 + b2

def linear_recurrence(a, b, h0):
    b = b.at[:, 0].add(a[:, 0] * h0)
    _, h = lax.associative_scan(_lin_combine, (a, b), axis=1)
    return h, h[:, -1]

def rglru_block(x, p, i, conv_prev, h_prev):
    bsz, t, _ = x.shape
    h = rmsnorm(x, p["norm_a_g"][i])
    proj = jnp.einsum("btd,de->bte", h, p["w_a_in"][i])
    gate_branch, rec = proj[..., :D_RNN], proj[..., D_RNN:]
    xc, conv_new = causal_dwconv(rec, conv_prev, p["conv_a_w"][i], p["conv_a_b"][i])
    gates = jnp.einsum("btnc,ncg->btng", xc.reshape(bsz, t, N_LRU_BLOCKS, LRU_BLOCK),
                       p["w_a_gate"][i]) + p["b_a_gate"][i]
    gates = jax.nn.sigmoid(gates.astype(jnp.float32))
    r = gates[..., :LRU_BLOCK].reshape(bsz, t, D_RNN)
    ig = gates[..., LRU_BLOCK:].reshape(bsz, t, D_RNN)
    log_a = LRU_C * r * jax.nn.log_sigmoid(p["lru_lambda"][i].astype(jnp.float32))
    a = jnp.exp(log_a)
    b = jnp.sqrt(-jnp.expm1(2.0 * log_a)) * ig * xc.astype(jnp.float32)
    hs, h_last = linear_recurrence(a, b, h_prev.astype(jnp.float32))
    y = hs.astype(x.dtype) * jax.nn.gelu(gate_branch, approximate=True)
    return x + jnp.einsum("btr,rd->btd", y, p["w_a_out"][i]), conv_new, h_last

def conv_ffn(x, p, l, prev):
    h = rmsnorm(x, p["norm_f_g"][l])
    proj = jnp.einsum("btd,de->bte", h, p["w_f_in"][l])
    gate, up = proj[..., :D_FF], proj[..., D_FF:]
    gate, conv_new = causal_dwconv(gate, prev, p["conv_f_w"][l], p["conv_f_b"][l])
    y = jax.nn.gelu(gate, approximate=True) * up
    return x + jnp.einsum("btf,fd->btd", y, p["w_f_out"][l]), conv_new

def shared_kv(x, p):
    bsz, t, _ = x.shape
    hd = N_HEADS * HEAD_DIM
    h = rmsnorm(x, p["norm_kv_g"])
    proj = jnp.einsum("btd,de->bte", h, p["w_kv"])
    k = proj[..., :hd].reshape(bsz, t, N_HEADS, HEAD_DIM)
    v = proj[..., hd:2 * hd].reshape(bsz, t, N_HEADS, HEAD_DIM)
    logf = jax.nn.log_sigmoid(proj[..., 2 * hd:].astype(jnp.float32) + p["b_forget"].astype(jnp.float32))
    return k, v, logf

def fox_attention(x, p, j, k, v, fk, fq, kpos, qpos):
    bsz, t, _ = x.shape
    h = rmsnorm(x, p["norm_b_g"][j])
    q = jnp.einsum("btd,de->bte", h, p["w_q"][j]).reshape(bsz, t, N_HEADS, HEAD_DIM)
    qb = min(Q_BLOCK, t)
    nqb = t // qb
    q_blocks = q.reshape(bsz, nqb, qb, N_HEADS, HEAD_DIM).transpose(1, 0, 2, 3, 4)
    fq_blocks = fq.reshape(bsz, nqb, qb, N_HEADS).transpose(1, 0, 3, 2)
    pos_blocks = qpos.reshape(nqb, qb)
    fk_t = jnp.swapaxes(fk, 1, 2)
    scale = HEAD_DIM ** -0.5

    def one_block(args):
        q_blk, fq_blk, pos_blk = args
        s = jnp.einsum("bqhd,bkhd->bhqk", q_blk, k, preferred_element_type=jnp.float32) * scale
        s = s + fq_blk[..., :, None] - fk_t[:, :, None, :]
        mask = kpos[None, :] <= pos_blk[:, None]
        s = jnp.where(mask, s, -jnp.inf)
        pr = jax.nn.softmax(s, axis=-1)
        return jnp.einsum("bhqk,bkhd->bqhd", pr.astype(v.dtype), v)

    o = lax.map(one_block, (q_blocks, fq_blocks, pos_blocks))
    o = o.transpose(1, 0, 2, 3, 4).reshape(bsz, t, N_HEADS * HEAD_DIM)
    return x + jnp.einsum("bte,ed->btd", o, p["w_o"][j])

def trunk(x, lru_h0, lru_conv0, ffn_conv0, past, p):
    lru_h_new, lru_conv_new, ffn_conv_new = [], [], []
    layer = 0
    for i in range(N_A_LAYERS):
        x, c_new, h_new = rglru_block(x, p, i, lru_conv0[i], lru_h0[i])
        x, f_new = conv_ffn(x, p, layer, ffn_conv0[layer])
        lru_h_new.append(h_new)
        lru_conv_new.append(c_new)
        ffn_conv_new.append(f_new)
        layer += 1
    k_new, v_new, logf_new = shared_kv(x, p)
    if past is None:
        k_all, v_all, logf_all = k_new, v_new, logf_new
    else:
        k_all = jnp.concatenate([past[0], k_new.astype(past[0].dtype)], axis=1)
        v_all = jnp.concatenate([past[1], v_new.astype(past[1].dtype)], axis=1)
        logf_all = jnp.concatenate([past[2].astype(jnp.float32), logf_new], axis=1)
    f_cum = jnp.cumsum(logf_all, axis=1)
    t = x.shape[1]
    tk = k_all.shape[1]
    kpos = jnp.arange(tk, dtype=jnp.int32)
    qpos = kpos[tk - t:]
    fq = f_cum[:, tk - t:]
    for j in range(N_B_LAYERS):
        x = fox_attention(x, p, j, k_all, v_all, f_cum, fq, kpos, qpos)
        x, f_new = conv_ffn(x, p, layer, ffn_conv0[layer])
        ffn_conv_new.append(f_new)
        layer += 1
    y = rmsnorm(x, p["norm_out_g"])
    return (y, k_new, v_new, logf_new, jnp.stack(lru_h_new, axis=0),
            jnp.stack(lru_conv_new, axis=0), jnp.stack(ffn_conv_new, axis=0))

def setup_inputs(seed: int = 0) -> dict:
    key = jax.random.key(seed)
    ks = jax.random.split(key, 32)
    f32 = jnp.float32

    def nrm(k, shape, scale=1.0):
        return jax.random.normal(k, shape, f32) * scale

    n_pages = PAST_LEN // PAGE_SIZE
    n_used = DEC_BATCH * n_pages
    n_phys = n_used + max(1, n_used // 4)
    hd = N_HEADS * HEAD_DIM
    page_table = jax.random.permutation(ks[0], n_phys)[:n_used].reshape(DEC_BATCH, n_pages).astype(jnp.int32)
    u = jax.random.uniform(ks[1], (N_A_LAYERS, D_RNN), f32, minval=0.9, maxval=0.999)
    s = u ** (1.0 / LRU_C)
    lru_lambda = jnp.log(s) - jnp.log1p(-s)
    return {
        "x_prompt": nrm(ks[2], (BATCH, SEQ, D_MODEL)),
        "x_sample": nrm(ks[3], (DEC_BATCH, DEC_SEQ, D_MODEL)),
        "cache_k": nrm(ks[4], (n_phys, PAGE_SIZE, N_HEADS, HEAD_DIM)),
        "cache_v": nrm(ks[5], (n_phys, PAGE_SIZE, N_HEADS, HEAD_DIM)),
        "cache_logf": jax.nn.log_sigmoid(FORGET_BIAS_OFFSET + nrm(ks[6], (n_phys, PAGE_SIZE, N_HEADS))),
        "state_lru_h": nrm(ks[7], (N_A_LAYERS, DEC_BATCH, D_RNN), 0.5),
        "state_lru_conv": nrm(ks[8], (N_A_LAYERS, DEC_BATCH, CONV_A_WIDTH - 1, D_RNN)),
        "state_ffn_conv": nrm(ks[9], (DEPTH, DEC_BATCH, CONV_F_WIDTH - 1, D_FF)),
        "page_table": page_table,
        "norm_a_g": 1.0 + nrm(ks[10], (N_A_LAYERS, D_MODEL), 0.05),
        "w_a_in": nrm(ks[11], (N_A_LAYERS, D_MODEL, 2 * D_RNN), D_MODEL ** -0.5),
        "conv_a_w": nrm(ks[12], (N_A_LAYERS, CONV_A_WIDTH, D_RNN), CONV_A_WIDTH ** -0.5),
        "conv_a_b": nrm(ks[13], (N_A_LAYERS, D_RNN), 0.01),
        "w_a_gate": nrm(ks[14], (N_A_LAYERS, N_LRU_BLOCKS, LRU_BLOCK, 2 * LRU_BLOCK), LRU_BLOCK ** -0.5),
        "b_a_gate": nrm(ks[15], (N_A_LAYERS, N_LRU_BLOCKS, 2 * LRU_BLOCK), 0.01),
        "lru_lambda": lru_lambda,
        "w_a_out": nrm(ks[16], (N_A_LAYERS, D_RNN, D_MODEL), D_RNN ** -0.5),
        "norm_f_g": 1.0 + nrm(ks[17], (DEPTH, D_MODEL), 0.05),
        "w_f_in": nrm(ks[18], (DEPTH, D_MODEL, 2 * D_FF), D_MODEL ** -0.5),
        "conv_f_w": nrm(ks[19], (DEPTH, CONV_F_WIDTH, D_FF), CONV_F_WIDTH ** -0.5),
        "conv_f_b": nrm(ks[20], (DEPTH, D_FF), 0.01),
        "w_f_out": nrm(ks[21], (DEPTH, D_FF, D_MODEL), D_FF ** -0.5),
        "norm_kv_g": 1.0 + nrm(ks[22], (D_MODEL,), 0.05),
        "w_kv": nrm(ks[23], (D_MODEL, 2 * hd + N_HEADS), D_MODEL ** -0.5),
        "b_forget": FORGET_BIAS_OFFSET + nrm(ks[24], (N_HEADS,), 0.5),
        "norm_b_g": 1.0 + nrm(ks[25], (N_B_LAYERS, D_MODEL), 0.05),
        "w_q": nrm(ks[26], (N_B_LAYERS, D_MODEL, hd), D_MODEL ** -0.5),
        "w_o": nrm(ks[27], (N_B_LAYERS, hd, D_MODEL), hd ** -0.5),
        "norm_out_g": 1.0 + nrm(ks[28], (D_MODEL,), 0.05),
    }

def reference(x_prompt, x_sample, cache_k, cache_v, cache_logf, state_lru_h, state_lru_conv,
              state_ffn_conv, page_table, norm_a_g, w_a_in, conv_a_w, conv_a_b, w_a_gate, b_a_gate,
              lru_lambda, w_a_out, norm_f_g, w_f_in, conv_f_w, conv_f_b, w_f_out, norm_kv_g, w_kv,
              b_forget, norm_b_g, w_q, w_o, norm_out_g):
    p = dict(norm_a_g=norm_a_g, w_a_in=w_a_in, conv_a_w=conv_a_w, conv_a_b=conv_a_b,
             w_a_gate=w_a_gate, b_a_gate=b_a_gate, lru_lambda=lru_lambda, w_a_out=w_a_out,
             norm_f_g=norm_f_g, w_f_in=w_f_in, conv_f_w=conv_f_w, conv_f_b=conv_f_b, w_f_out=w_f_out,
             norm_kv_g=norm_kv_g, w_kv=w_kv, b_forget=b_forget, norm_b_g=norm_b_g, w_q=w_q, w_o=w_o,
             norm_out_g=norm_out_g)

    bsz = x_prompt.shape[0]
    h0 = jnp.zeros((N_A_LAYERS, bsz, D_RNN), jnp.float32)
    c0 = jnp.zeros((N_A_LAYERS, bsz, CONV_A_WIDTH - 1, D_RNN), x_prompt.dtype)
    f0 = jnp.zeros((DEPTH, bsz, CONV_F_WIDTH - 1, D_FF), x_prompt.dtype)
    (y_prompt, k_prompt, v_prompt, logf_prompt, lru_h_prompt, lru_conv_prompt,
     ffn_conv_prompt) = trunk(x_prompt, h0, c0, f0, None, p)

    dec_batch = x_sample.shape[0]
    past_len = page_table.shape[1] * cache_k.shape[1]
    k_past = cache_k[page_table].reshape(dec_batch, past_len, N_HEADS, HEAD_DIM)
    v_past = cache_v[page_table].reshape(dec_batch, past_len, N_HEADS, HEAD_DIM)
    logf_past = cache_logf[page_table].reshape(dec_batch, past_len, N_HEADS)
    (y_sample, k_sample, v_sample, logf_sample, lru_h_sample, lru_conv_sample,
     ffn_conv_sample) = trunk(x_sample, state_lru_h, state_lru_conv, state_ffn_conv,
                              (k_past, v_past, logf_past), p)

    return (y_prompt, y_sample, k_prompt, v_prompt, logf_prompt, lru_h_prompt, lru_conv_prompt,
            ffn_conv_prompt, k_sample, v_sample, logf_sample, lru_h_sample, lru_conv_sample,
            ffn_conv_sample)


_drawn_inputs = setup_inputs


def setup_inputs(seed=0):
    import zlib

    import numpy as np

    out = dict(_drawn_inputs(seed))
    spreads = {}
    factors = {'b_a_gate': 8.0, 'conv_f_b': 7.586, 'norm_b_g': 5.232}
    for name, (base, spread) in spreads.items():
        noise = np.random.default_rng([zlib.crc32(name.encode()), seed]).standard_normal(out[name].shape)
        drawn = base * np.exp(spread * noise) if base else spread * noise
        out[name] = __import__('jax').numpy.asarray(drawn.astype(out[name].dtype))
    for name, factor in factors.items():
        out[name] = (out[name] * factor).astype(out[name].dtype)
    return out
```

```python
from contextlib import ExitStack

import numpy as np

import concourse.bass as bass
from concourse import mybir

F32 = mybir.dt.float32
F32R = mybir.dt.float32r
BF16 = mybir.dt.bfloat16
I32 = mybir.dt.int32
ALU = mybir.AluOpType
ACT = mybir.ActivationFunctionType

P = 128
D = 1024
KT = D // P
SEQ = 1024
DB, DS = 8, 4
NS = DB * DS
T = SEQ + NS
CH = T // 3
TAIL = SEQ - 2 * CH
NH, HD = 16, 64
NHP = NH // 2
PAST, PAGE = 256, 128
NPG = PAST // PAGE
DF = 3 * D
FT = 6
FSTEPS = DF // P // FT
FJ = 2 * FT + KT
NQB = SEQ // P
WA, WF = 4, 3
EPS = 1e-6
NEG = -3.0e38
SCALE = HD ** -0.5
DK = PAST + NS
POOL_TILES = 3
B_CONSTS = 6 + DB * NPG
UNITS = 1 + 2 * NQB

J_REC, J_BR, J_AOUT, J_F0 = 0, KT, 2 * KT, 3 * KT
J_FG = J_F0 + FSTEPS * FJ
J_QKV = J_FG + 1
J_O = J_QKV + 3 * NHP
J_F1 = J_O + KT
J_END = J_F1 + FSTEPS * FJ

BLOCKS = [7, 0, 6, 1, 5, 2, 4, 3]
UNIT_OF = [None] + [(h, i) for h in range(2) for i in BLOCKS]
SPLIT_SLOTS = [1, 7, 14]
KSTEPS = [2, 1, 2] + [1] * 14 + [3, 2]


def hybrid_step_kernel(nc, ins, outs):
    ctx = ExitStack()
    with ctx:
        base = (nc.sbuf_base + 31) // 32 * 32
        end = [base]

        def at(name, shape, dt, offset):
            return nc.alloc_sbuf_tensor_at(name, shape, dt, offset=offset)

        def region(floats):
            o = end[0]
            end[0] = o + (floats * 4 + 31) // 32 * 32
            assert end[0] <= nc.sbuf_usable_end, (end[0], nc.sbuf_usable_end)
            return o

        def sem(name):
            return ctx.enter_context(nc.semaphore(name))

        X = at("X", [P, KT, T], F32, region(KT * T))
        XH = at("XH", [P, KT, T], F32R, region(KT * T))
        XL = at("XL", [P, KT, T], F32R, region(KT * T))
        o_y = region(2 * KT * T)
        end_y = o_y + 8 * KT * T
        YH = at("YH", [P, KT, T], F32R, o_y)
        YL = at("YL", [P, KT, T], F32R, o_y + 4 * KT * T)
        WR = at("WR", [P, 2, KT * P], F32, region(2 * KT * P))
        WH = at("WH", [P, 2, KT * P], F32R, region(2 * KT * P))
        WL = at("WL", [P, 2, KT * P], F32R, region(2 * KT * P))
        RS = at("RS", [P, T], F32, region(T))
        o_u = region(2 * T)
        U = at("U", [P, 2, T], F32, o_u)
        gains = at("gains", [P, 6, KT], F32, region(6 * KT))
        ones = at("ones", [P, P], F32, region(P))
        ident = at("ident", [P, P], F32, region(P))
        cvec = at("cvec", [P, 2], F32, region(8))
        ptab = at("ptab", [1, DB * NPG], I32, region(16))
        o_c = region(800)
        o_s = region(488)

        def lay(o, name, shape, dt):
            words = int(np.prod(shape[1:]))
            return at(name, shape, dt, o), o + (4 * words + 31) // 32 * 32

        RW = SEQ + WA - 1 + DB * (DS + WA - 1)
        CW = RW - (WA - 1)
        o = o_y
        RB, o_xc = lay(o, "RB", [P, 2, RW], F32)
        XC, o = lay(o_xc, "XC", [P, 2, RW], F32)
        GR = at("GR", [P, 2, T], F32, o); o += 8 * T
        GI = at("GI", [P, 2, T], F32, o); o += 8 * T
        TM = at("TM", [P, 2, T], F32, o); o += 8 * T
        XCH = at("XCH", [P, T], F32R, o); o += 4 * T
        XCL = at("XCL", [P, T], F32R, o); o += 4 * T
        GWH = at("GWH", [P, KT, 2 * P], F32R, o); o += 8 * KT * P
        GWL = at("GWL", [P, KT, 2 * P], F32R, o); o += 8 * KT * P
        assert o <= end_y
        GWR = at("GWR", [P, KT, 2 * P], F32, o_u)
        hS = at("hS", [P, KT, DB, DS + 1], F32, o_xc)
        aS = at("aS", [P, KT, DB, DS + 1], F32, o_c)
        bS = at("bS", [P, KT, DB, DS + 1], F32, o_c + 4 * 320)
        apar = at("apar", [P, KT, 8], F32, o_s)
        clam = at("clam", [P, KT, 2], F32, o_s + 4 * 64)
        cst = at("cst", [P, KT, DB, WA - 1], F32, o_s + 4 * 80)
        cop = at("cop", [P, KT, WA - 1], F32, o_s + 4 * 272)
        cos = at("cos", [P, KT, DB, WA - 1], F32, o_s + 4 * 296)
        hl = at("hl", [P, KT, 1 + DB], F32, o_s + 4 * 80)

        FYH = at("FYH", [P, FT, T], F32R, o_y)
        FYL = at("FYL", [P, FT, T], F32R, o_y + 4 * FT * T)
        GW = SEQ + WF - 1 + DB * (DS + WF - 1)
        FW = GW - (WF - 1)
        o = o_y + 8 * FT * T
        GB, o = lay(o, "GB", [P, GW], F32)
        CB, o = lay(o, "CB", [P, 2, GW], F32)
        assert o <= end_y
        fpar = at("fpar", [P, FT, 4], F32, o_s)
        fst = at("fst", [P, FT, DB, WF - 1], F32, o_s + 4 * 24)
        fop = at("fop", [P, FT, WF - 1], F32, o_s + 4 * 120)
        fos = at("fos", [P, FT, DB, WF - 1], F32, o_s + 4 * 136)

        o = o_y
        QS = at("QS", [P, T], F32, o); o += 4 * T
        KS = at("KS", [P, T], F32, o); o += 4 * T
        VS = at("VS", [P, T], F32, o); o += 4 * T
        QH = at("QH", [P, SEQ], F32R, o); o += 4 * SEQ
        QL = at("QL", [P, SEQ], F32R, o); o += 4 * SEQ
        KH = at("KH", [P, SEQ], F32R, o); o += 4 * SEQ
        KL = at("KL", [P, SEQ], F32R, o); o += 4 * SEQ
        VH = at("VH", [P, NQB, P], F32R, o); o += 4 * SEQ
        VL = at("VL", [P, NQB, P], F32R, o); o += 4 * SEQ
        SB = at("SB", [P, 2, SEQ], F32, o); o += 8 * SEQ
        o_p = o
        PTH = at("PTH", [P, 2, SEQ], F32R, o); o += 8 * SEQ
        PTL = at("PTL", [P, 2, SEQ], F32R, o); o += 8 * SEQ
        NF = at("NF", [P, SEQ], F32, o); o += 4 * SEQ
        DFc = at("DFc", [P, DK], F32, o); o += 4 * DK
        SEL = at("SEL", [P, 2 * NS], F32, o); o += 8 * NS
        QD = at("QD", [P, DB, 2, DS], F32, o); o += 8 * NS
        assert o <= end_y
        CC = at("CC", [P, DB, PAST], F32, o_u)
        QXd = at("QXd", [P, DB, DB * 2 * DS + 2 * DS], F32, o_c)
        QX = QXd[:, :, :].rearrange("p a b -> p (a b)")[:, 0:2 * NS * DB].rearrange("p (b c) -> p b c", b=DB)
        DM = at("DM", [2 * NS, DK], F32, o_c + 4 * 576)
        VN = at("VN", [NS, P], F32, o_p + 12 * SEQ)
        PTD = at("PTD", [P, 3 * 2 * NS], F32, o_p + 12 * SEQ + 4 * 256)
        C0 = at("C0", [P, DK], F32, o_p)
        C1 = at("C1", [P, DK], F32, o_p + 4 * DK)
        CN = at("CN", [NS, DK], F32, o_p + 8 * DK)
        LP = at("LP", [P, NPG, DB, NH], F32, o_p + 12 * DK)
        LNX = at("LNX", [NS, DB, NH], F32, o_p + 12 * DK + 4 * 256)
        ON16 = at("ON16", [NH, SEQ], F32, o_p + 12 * DK + 4 * 384)
        maskF = at("maskF", [P, P], F32, o_p + 12 * DK + 4 * (384 + SEQ))
        o_t = o_c + 4 * 864
        nmax = at("nmax", [P, UNITS], F32, o_t)
        lsum = at("lsum", [P, UNITS], F32, o_t + 4 * 32)
        linv = at("linv", [P, UNITS], F32, o_t + 4 * 64)
        bfg = at("bfg", [NH, 1], F32, o_t + 4 * 96)
        identB = at("identB", [P, P], BF16, o_t + 4 * 128)
        maskB = at("maskB", [P, P], BF16, o_t + 4 * 192)

        psum = ctx.enter_context(nc.psum_tensor("psum", [P, 8, 512], F32))

        def acc(slot):
            return psum[:, 3 * slot:3 * slot + 3, 0:CH]

        S_ps = psum[:, 3:5, :].rearrange("p a b -> p (a b)")
        T_ps = psum[:, 5:7, :].rearrange("p a b -> p (a b)")
        O_ps = psum[:, 7, :]

        gain_ld, ones_ld, const_ld, gw_ld = sem("gain_ld"), sem("ones_ld"), sem("const_ld"), sem("gw_ld")
        x_ld = [sem(f"x_ld{n}") for n in range(KT)]
        raw_ld = [sem("raw_ld0"), sem("raw_ld1")]
        w_gained, w_hi, w_ready = sem("w_gained"), sem("w_hi"), sem("w_ready")
        job_done, acc_read = sem("job_done"), sem("acc_read")
        x_hi, x_lo, sq_done, sq_sum = sem("x_hi"), sem("x_lo"), sem("sq_done"), sem("sq_sum")
        ms_done, sqrt_done, rstd_ready = sem("ms_done"), sem("sqrt_done"), sem("rstd_ready")
        gw_hi, gw_lo, lam_step = sem("gw_hi"), sem("gw_lo"), sem("lam_step")
        a_pad, a_win, a_rows, a_conv = sem("a_pad"), sem("a_win"), sem("a_rows"), sem("a_conv")
        xc_done, xc_hi, xc_lo = sem("xc_done"), sem("xc_hi"), sem("xc_lo")
        gate_mm, gate_rd = sem("gate_mm"), sem("gate_rd")
        tanh_done, a0_done, m_done, mm2_done = sem("tanh_done"), sem("a0_done"), sem("m_done"), sem("mm2_done")
        a_done, root_done, ix_done, b_done = sem("a_done"), sem("root_done"), sem("ix_done"), sem("b_done")
        scan_done, hs_done, h_dec = sem("scan_done"), sem("hs_done"), sem("h_dec")
        br_gelu, y_done, y_hi, y_lo = sem("br_gelu"), sem("y_done"), sem("y_hi"), sem("y_lo")
        a_out = sem("a_out")
        f_pad, f_par, f_win, f_rows = sem("f_pad"), sem("f_par"), sem("f_win"), sem("f_rows")
        f_c1, f_c2, f_c3, f_gelu = sem("f_c1"), sem("f_c2"), sem("f_c3"), sem("f_gelu")
        h_done, h_hi, h_lo, f_out = sem("h_done"), sem("h_hi"), sem("h_lo"), sem("f_out")
        b_const, fg_one, fg_step, fg_act = sem("b_const"), sem("fg_one"), sem("fg_step"), sem("fg_act")
        lf_ready, lf_out, nf_out = sem("lf_ready"), sem("lf_out"), sem("nf_out")
        lnt, lnx, df_mm, df_rd, qx_zero = sem("lnt"), sem("lnx"), sem("df_mm"), sem("df_rd"), sem("qx_zero")
        nf_ld, sel_ld, mask_ready = sem("nf_ld"), sem("sel_ld"), sem("mask_ready")
        logits_seen, probs_seen = sem("logits_seen"), sem("probs_seen")
        cc_ld = [sem(f"cc_ld{b}") for b in range(DB)]
        q_hi, q_lo, k_hi, k_lo, qd_done = sem("q_hi"), sem("q_lo"), sem("k_hi"), sem("k_lo"), sem("qd_done")
        v_t, v_hi, v_lo, vn_rd = sem("v_t"), sem("v_hi"), sem("v_lo"), sem("vn_rd")
        qk_done, s_read, e_done, rl_done = sem("qk_done"), sem("s_read"), sem("e_done"), sem("rl_done")
        p_norm, t_done, pt_hi, pt_lo = sem("p_norm"), sem("t_done"), sem("pt_hi"), sem("pt_lo")
        pv_done, o_read, k_out, v_out = sem("pv_done"), sem("o_read"), sem("k_out"), sem("v_out")
        o_hi, o_lo, res_done = sem("o_hi"), sem("o_lo"), sem("res_done")
        y_gained, yp_done = sem("y_gained"), sem("yp_done")
        yo_done, y_out = sem("yo_done"), sem("y_out")

        def wait(eng, s, v):
            if not isinstance(v, int) or v > 0:
                eng.wait_ge(s, v)

        def wait_apart(eng, s, v, seen):
            eng.wait_ge(s, v)
            if not isinstance(v, int):
                eng.sem_inc(seen, 1)

        def fixed(first, per, step):
            return (first + per * step, 0, 0) if isinstance(step, int) else (first, per, step)

        def shape_of(J):
            for f in (J_F0, J_F1):
                if f <= J < f + FSTEPS * FJ:
                    return (KT * P if (J - f) % FJ < 2 * FT else FT * P), False
            if J == J_FG:
                return KT * NH, True
            return KT * P, J_QKV <= J < J_O

        def load_weights(sp, src, first, per=0, step=0):
            first, per, step = fixed(first, per, step)
            J, par, (n, _) = first + per * step, first % 2, shape_of(first)
            wait(sp, w_ready, J - 1)
            sp.dma_start(WR[:, par, 0:n], src).then_inc(raw_ld[par], 16)

        def hi_weights(act, first, per=0, step=0):
            first, per, step = fixed(first, per, step)
            if first >= J_END:
                return
            J, par, (n, gained) = first + per * step, first % 2, shape_of(first)
            if gained:
                act.wait_ge(w_gained, J - J_FG + 1)
            else:
                act.wait_ge(raw_ld[par], 16 * (first // 2 + 1 + per // 2 * step))
            wait(act, job_done, J - 1)
            nc.scalar.activation(WH[:, par, 0:n], WR[:, par, 0:n], ACT.Copy).then_inc(w_hi, 1)

        def lo_weights(dve, first, per=0, step=0):
            first, per, step = fixed(first, per, step)
            if first >= J_END:
                return
            J, par, (n, _) = first + per * step, first % 2, shape_of(first)
            dve.wait_ge(w_hi, J + 1)
            nc.vector.tensor_tensor(WL[:, par, 0:n], WR[:, par, 0:n], WH[:, par, 0:n].bitcast(F32),
                                    ALU.subtract).then_inc(w_ready, 1)

        def k_step(k, slot, wslot, xh, xl, nk, m=P):
            wh = WH[:, wslot, k * m:(k + 1) * m]
            wl = WL[:, wslot, k * m:(k + 1) * m]
            for w, x, part in ((wh, xh, 0), (wh, xl, 1), (wl, xh, 2)):
                for c in range(3):
                    mm = nc.tensor.matmul(psum[0:m, 3 * slot + c, 0:CH], w, x[:, k, c * CH:(c + 1) * CH],
                                          start=(k == 0 and part == 0), stop=(k == nk - 1 and part == 2),
                                          skip_group_check=True)
            return mm

        def job(pe, first, per, step, xh, xl, nk=KT, before_k=None, after_k=None, m=P):
            J, par = first + per * step, first % 2
            pe.wait_ge(w_ready, J + 1)
            wait(pe, acc_read, J - 1)
            for k in range(nk):
                if before_k:
                    before_k(k)
                mm = k_step(k, par, par, xh, xl, nk, m)
                if k == nk - 1:
                    mm.then_inc(job_done, 1)
                if after_k:
                    after_k(k)

        def square_to(d):
            return RS[:, :] if d == 0 else U[:, d % 2, :]

        def split_hi(act, p, d, ready, value, gain=None, split=True):
            act.wait_ge(ready, value)
            if split and gain is None:
                nc.scalar.activation(XH[:, d, :], X[:, d, :], ACT.Copy).then_inc(x_hi, 1)
            elif split:
                nc.scalar.activation(XH[:, d, :], X[:, d, :], ACT.Identity,
                                     scale=gains[:, gain, d:d + 1]).then_inc(x_hi, 1)
            if d >= 3:
                act.wait_ge(sq_sum, 7 * p + d - 2)
            nc.scalar.activation(square_to(d), X[:, d, :], ACT.Square).then_inc(sq_done, 1)

        def split_lo(dve, p, d, gain=None):
            dve.wait_ge(x_hi, KT * p + d + 1)
            if gain is None:
                ins_ = nc.vector.tensor_tensor(XL[:, d, :], X[:, d, :], XH[:, d, :].bitcast(F32), ALU.subtract)
            else:
                ins_ = nc.vector.scalar_tensor_tensor(XL[:, d, :], X[:, d, :], gains[:, gain, d:d + 1],
                                                      XH[:, d, :].bitcast(F32), ALU.mult, ALU.subtract)
            ins_.then_inc(x_lo, 1)

        def add_square(pool, p, d):
            pool.wait_ge(sq_done, KT * p + d + 1)
            if d >= 2:
                pool.wait_ge(sq_sum, 7 * p + d - 1)
            nc.gpsimd.tensor_tensor(RS[:, :], RS[:, :], square_to(d), ALU.add).then_inc(sq_sum, 1)

        def sum_squares(pool, p):
            for d in range(1, KT):
                add_square(pool, p, d)

        PIECES = [(6, 0, 512), (7, 512, SEQ), (6, SEQ, T)]

        def mean_square(pe, p):
            pe.wait_ge(sq_sum, 7 * (p + 1))
            for c, (bank, a, b) in enumerate(PIECES):
                if c == 2:
                    pe.wait_ge(sqrt_done, 3 * p + 1)
                nc.tensor.matmul(psum[:, bank, 0:b - a], ones[:, :], RS[:, a:b],
                                 start=True, stop=True).then_inc(ms_done, 1)

        def root(act, p):
            for c, (bank, a, b) in enumerate(PIECES):
                act.wait_ge(ms_done, 3 * p + c + 1)
                nc.scalar.activation(RS[:, a:b], psum[:, bank, 0:b - a], ACT.Sqrt,
                                     bias=cvec[:, 0:1]).then_inc(sqrt_done, 1)

        def inverse(dve, p):
            for c, (_, a, b) in enumerate(PIECES):
                dve.wait_ge(sqrt_done, 3 * p + c + 1)
                nc.vector.reciprocal(RS[:, a:b], RS[:, a:b]).then_inc(rstd_ready, 1)
            dve.wait_ge(rstd_ready, 3 * (p + 1))

        def thirds(x):
            return x.rearrange("p (a b) -> p a b", a=3)

        def windows(x, start, rows):
            return x[:, start:start + DB * rows].rearrange("p (b r) -> p b r", r=rows)

        def scaled_in(dve, slot, buf, pad, rows):
            nc.vector.tensor_tensor(buf[:, pad:pad + 2 * CH].rearrange("p (a b) -> p a b", a=2),
                                    psum[:, 3 * slot:3 * slot + 2, 0:CH],
                                    RS[:, 0:2 * CH].rearrange("p (a b) -> p a b", a=2), ALU.mult)
            nc.vector.tensor_tensor(buf[:, pad + 2 * CH:pad + SEQ], psum[:, 3 * slot + 2, 0:TAIL],
                                    RS[:, 2 * CH:SEQ], ALU.mult)
            return nc.vector.tensor_tensor(
                windows(buf, pad + SEQ, rows)[:, :, pad:rows],
                psum[:, 3 * slot + 2, TAIL:CH].rearrange("p (b r) -> p b r", r=DS),
                RS[:, SEQ:T].rearrange("p (b r) -> p b r", r=DS), ALU.mult)

        def scaled(dve, slot, out):
            return nc.vector.tensor_tensor(thirds(out), acc(slot), thirds(RS[:, :]), ALU.mult)

        def i_times_xc(pool, n):
            pool.wait_ge(gate_rd, 6 * (n + 1))
            nc.gpsimd.tensor_tensor(GI[:, n % 2, :], GI[:, n % 2, :], XC[:, n % 2, 0:T],
                                    ALU.mult).then_inc(ix_done, 1)

        def decay_of_state(pool, n):
            pool.wait_ge(mm2_done, n + 1)
            nc.gpsimd.tensor_scalar(aS[:, n, :, 1:], TM[:, n % 2, SEQ:T].rearrange("p (b r) -> p b r", r=DS),
                                    -1.0, 1.0, ALU.mult, ALU.add).then_inc(a_done, 1)
            nc.gpsimd.tensor_scalar(TM[:, n % 2, 0:SEQ], TM[:, n % 2, 0:SEQ], -1.0, 1.0,
                                    ALU.mult, ALU.add).then_inc(a_done, 1)

        def input_of_state(pool, n):
            pool.wait_ge(root_done, n + 1)
            pool.wait_ge(ix_done, n + 1)
            nc.gpsimd.tensor_tensor(bS[:, n, :, 1:], GI[:, n % 2, SEQ:T].rearrange("p (b r) -> p b r", r=DS),
                                    GR[:, n % 2, SEQ:T].rearrange("p (b r) -> p b r", r=DS),
                                    ALU.mult).then_inc(b_done, 1)
            nc.gpsimd.tensor_tensor(GI[:, n % 2, 0:SEQ], GI[:, n % 2, 0:SEQ], GR[:, n % 2, 0:SEQ],
                                    ALU.mult).then_inc(b_done, 1)

        block = ctx.enter_context(nc.Block())

        @block.sync
        def _(sp):
            for n in range(KT):
                sp.dma_start(X[:, n, :], ins["xT"][n]).then_inc(x_ld[n], 16)
                if n == 0:
                    sp.dma_start(gains[:, :, :], ins["gains"]).then_inc(gain_ld, 16)
                    sp.dma_start(ones[:, :], ins["ones"]).then_inc(ones_ld, 16)
                    sp.dma_start(cvec[:, :], ins["cvec"]).then_inc(ones_ld, 16)
                    load_weights(sp, ins["wa"][0], 0)
            load_weights(sp, ins["wa"][1], 1)
            sp.dma_start(apar[:, :, :], ins["apar"]).then_inc(const_ld, 16)
            sp.dma_start(cst[:, :, :, :], ins["conv_state"]).then_inc(const_ld, 16)
            sp.dma_start(bS[:, :, :, :], ins["h0"]).then_inc(const_ld, 16)
            sp.dma_start(ident[:, :], ins["ident"]).then_inc(const_ld, 16)
            sp.dma_start(ptab[:, :], ins["pages"]).then_inc(const_ld, 16)
            sp.wait_ge(sq_sum, 7)
            sp.dma_start(GWR[:, :, :], ins["wg"]).then_inc(gw_ld, 16)
            for J in range(2, J_F0):
                load_weights(sp, ins["wa"][J], J)
                n = J - 12
                if 0 <= n < KT:
                    sp.wait_ge(y_done, n + 1)
                    sp.dma_start(X[:, n, :], ins["xT"][n]).then_inc(x_ld[n], 16)
            sp.wait_ge(a_rows, 2 * KT)
            sp.wait_ge(h_dec, 3)
            sp.dma_start(outs["conv_p"], cop[:, :, :]).then_inc(a_out, 16)
            sp.dma_start(outs["conv_s"], cos[:, :, :, :]).then_inc(a_out, 16)
            sp.dma_start(outs["hlast"], hl[:, :, :]).then_inc(a_out, 16)
            sp.wait_ge(a_out, 48)

            def ffn(L, step):
                first, fs = (J_F0, J_F1)[L], L * FSTEPS + step
                wait(sp, f_c3, 2 * FT * fs)
                sp.dma_start(fpar[:, :, :], ins["fpar"][L, step]).then_inc(f_par, 16)
                sp.dma_start(fst[:, :, :, :], ins["fst"][L, step]).then_inc(f_par, 16)
                for j in range(2 * FT):
                    load_weights(sp, ins["wfi"][L, step, j], first + j, FJ, step)
                for d in range(KT):
                    load_weights(sp, ins["wfo"][L, step, d], first + 2 * FT + d, FJ, step)
                    if d == 1:
                        sp.wait_ge(f_rows, 2 * FT * (fs + 1))
                        sp.dma_start(outs["ffn_p"][L, step], fop[:, :, :]).then_inc(f_out, 16)
                        sp.dma_start(outs["ffn_s"][L, step], fos[:, :, :, :]).then_inc(f_out, 16)

            ffn(0, 0)
            with sp.Fori(1, FSTEPS - 1) as step:
                ffn(0, step)
            ffn(0, FSTEPS - 1)

            load_weights(sp, ins["wfg"], J_FG)
            load_weights(sp, ins["wqkv"][0, 0], J_QKV)
            load_weights(sp, ins["wqkv"][0, 1], J_QKV + 1)
            sp.wait_ge(job_done, J_FG)
            sp.wait_ge(f_out, 32 * FSTEPS)
            for dst, name in ((C0, "c0"), (C1, "c1"), (CN, "cn"), (DM, "dm"), (bfg, "bfg"),
                              (maskF, "mask")):
                sp.dma_start(dst[:, :], ins[name]).then_inc(b_const, 16)
            load_weights(sp, ins["wqkv"][0, 2], J_QKV + 2)
            sp.wait_ge(const_ld, 80)
            page = [sp.value_load(ptab[0:1, j:j + 1], min_val=0, max_val=ins["clf"].shape[0] - 1)
                    for j in range(DB * NPG)]
            for b in range(DB):
                for g in range(NPG):
                    sp.dma_start(LP[:, g, b, :], ins["clf"][page[NPG * b + g]]).then_inc(b_const, 16)
            sp.wait_ge(sq_sum, 7 * 3)

            def load_cache(name, hp):
                for b in range(DB):
                    for g in range(NPG):
                        sp.dma_start(CC[:, b, g * PAGE:(g + 1) * PAGE],
                                     ins[name][page[NPG * b + g], hp]).then_inc(cc_ld[b], 16)

            load_cache("ck", 0)
            sp.dma_start(SEL[:, :], ins["sel"][0]).then_inc(sel_ld, 16)
            sp.wait_ge(lf_ready, 1)
            sp.dma_start(outs["logf"], VS[0:NH, :]).then_inc(lf_out, 16)
            sp.wait_ge(fg_step, 4)
            sp.dma_start(ins["nf"], KS[0:NH, 0:SEQ]).then_inc(nf_out, 16)
            sp.wait_ge(nf_out, 16)
            load_weights(sp, ins["wqkv"][1, 0], J_QKV + 3)
            sp.wait_ge(acc_read, J_QKV + 2)
            sp.dma_start(outs["k"][0], KS[:, :]).then_inc(k_out, 16)

            def pair(c, t):
                hp, u0, last = c + 2 * t, UNITS * c + 2 * UNITS * t, c == NHP - 1
                sp.wait_ge(acc_read, J_QKV + 3 * c + 3 + 6 * t)
                sp.dma_start(outs["v"][hp], VS[:, :]).then_inc(v_out, 16)
                wait(sp, s_read, u0)
                sp.dma_start(NF[:, :], ins["nf"][2 * hp, :].partition_broadcast(P)).then_inc(nf_ld, 16)
                if not last:
                    load_weights(sp, ins["wqkv"][hp + 1, 1], J_QKV + 3 * c + 4, 6, t)
                sp.wait_ge(qk_done, u0 + 1)
                load_cache("cv", hp)
                if not last:
                    sp.dma_start(SEL[:, :], ins["sel"][hp + 1]).then_inc(sel_ld, 16)
                    load_weights(sp, ins["wqkv"][hp + 1, 2], J_QKV + 3 * c + 5, 6, t)
                    sp.wait_ge(pv_done, u0 + 1)
                    load_cache("ck", hp + 1)
                sp.wait_ge(s_read, u0 + 1 + NQB)
                sp.dma_start(NF[:, :], ins["nf"][2 * hp + 1, :].partition_broadcast(P)).then_inc(nf_ld, 16)
                if c == NHP - 2:
                    load_weights(sp, ins["wo"][0], J_O)
                elif not last:
                    load_weights(sp, ins["wqkv"][hp + 2, 0], J_QKV + 3 * c + 6, 6, t)
                if not last:
                    sp.wait_ge(acc_read, J_QKV + 3 * c + 5 + 6 * t)
                    sp.dma_start(outs["k"][hp + 1], KS[:, :]).then_inc(k_out, 16)

            over_pairs(sp, pair)
            for d in range(1, KT):
                load_weights(sp, ins["wo"][d], J_O + d)
            sp.wait_ge(job_done, J_O + 1)
            ffn(1, 0)
            with sp.Fori(1, FSTEPS - 1) as step:
                ffn(1, step)
            ffn(1, FSTEPS - 1)
            for d in [3, 4, 0, 5, 6, 1, 7, 2]:
                if d < POOL_TILES:
                    sp.wait_ge(yp_done, d + 1)
                else:
                    sp.wait_ge(yo_done, d - POOL_TILES + 1)
                sp.dma_start(outs["y"][d], X[:, d, :]).then_inc(y_out, 16)
            sp.wait_ge(y_out, 16 * KT)
            sp.wait_ge(f_out, 64 * FSTEPS)
            sp.wait_ge(k_out, 16 * NHP)
            sp.wait_ge(v_out, 16 * NHP)
            sp.wait_ge(lf_out, 16)

        @block.gpsimd
        def _(pool):
            nc.gpsimd.memset(RB[:, :, 0:WA - 1], 0.0).then_inc(a_pad, 1)
            nc.gpsimd.memset(aS[:, :, :, 0:1], 0.0).then_inc(a_pad, 1)
            sum_squares(pool, 0)
            pool.wait_ge(const_ld, 80)

            def conv_rows(n):
                wait(pool, xc_done, 2 * (n - 1))
                nc.gpsimd.tensor_copy(windows(RB[:, n % 2, :], WA - 1 + SEQ, DS + WA - 1)[:, :, 0:WA - 1],
                                      cst[:, n, :, :]).then_inc(a_win, 1)

            conv_rows(0)
            conv_rows(1)
            for n in range(KT):
                pool.wait_ge(acc_read, J_REC + n + 1)
                nc.gpsimd.tensor_copy(cop[:, n, :], RB[:, n % 2, SEQ:SEQ + WA - 1]).then_inc(a_rows, 1)
                nc.gpsimd.tensor_copy(cos[:, n, :, :],
                                      windows(RB[:, n % 2, :], WA - 1 + SEQ, DS + WA - 1)[:, :, DS:]
                                      ).then_inc(a_rows, 1)
                if n >= 2:
                    i_times_xc(pool, n - 2)
                if n + 2 < KT:
                    conv_rows(n + 2)
                if n >= 2:
                    decay_of_state(pool, n - 2)
                    input_of_state(pool, n - 2)
            for n in (KT - 2, KT - 1):
                i_times_xc(pool, n)
                decay_of_state(pool, n)
                input_of_state(pool, n)
            sum_squares(pool, 1)

            pool.wait_ge(job_done, J_F0)
            nc.gpsimd.memset(GB[:, 0:WF - 1], 0.0).then_inc(f_pad, 1)
            def gain(first, per=0, t=0):
                par, (n, _) = first % 2, shape_of(first)
                w = WR[:, par, 0:n].rearrange("p (k m) -> p k m", k=KT)
                g = gains[:, 3 if first >= J_QKV and (first - J_QKV) % 3 == 0 else 2, :]
                pool.wait_ge(raw_ld[par], 16 * (first // 2 + 1 + per // 2 * t))
                nc.gpsimd.tensor_tensor(w, w, g.unsqueeze(2).to_broadcast([P, KT, n // KT]),
                                        ALU.mult).then_inc(w_gained, 1)

            for d in range(1, KT):
                if d >= KT - 2:
                    gain(J_FG + d - (KT - 2))
                add_square(pool, 2, d)
            gain(J_QKV + 1)
            nc.gpsimd.memset(ON16[:, :], 1.0).then_inc(fg_one, 1)
            pool.wait_ge(b_const, 16 * B_CONSTS)
            pool.wait_ge(const_ld, 80)
            nc.gpsimd.tensor_copy(identB[:, :], ident[:, :]).then_inc(mask_ready, 1)
            nc.gpsimd.tensor_copy(maskB[:, :], maskF[:, :]).then_inc(mask_ready, 1)
            gain(J_QKV + 2)
            gain(J_QKV + 3)

            def pair(c, t):
                for r in (4, 5, 6):
                    if J_QKV + 3 * c + r < J_O:
                        gain(J_QKV + 3 * c + r, 6, t)

            over_pairs(pool, pair)
            sum_squares(pool, 3)
            pool.wait_ge(job_done, J_F1)
            nc.gpsimd.memset(GB[:, 0:WF - 1], 0.0).then_inc(f_pad, 1)
            sum_squares(pool, 4)
            pool.wait_ge(rstd_ready, 15)
            for d in range(POOL_TILES):
                pool.wait_ge(y_gained, d + 1)
                nc.gpsimd.tensor_tensor(X[:, d, :], X[:, d, :], RS[:, :], ALU.mult).then_inc(yp_done, 1)

        @block.scalar
        def _(act):
            act.wait_ge(gain_ld, 16)
            for d in range(KT):
                split_hi(act, 0, d, x_ld[d], 16, gain=0)
                if d == 0:
                    hi_weights(act, 0)
            hi_weights(act, 1)
            act.wait_ge(ones_ld, 32)
            root(act, 0)
            for func, n in ((ACT.Exp, 1), (ACT.Ln, 2)):
                act.wait_ge(lam_step, n)
                nc.scalar.activation(clam[:, :, 0], clam[:, :, 0], func,
                                     bias=(0.0 if func == ACT.Exp else cvec[:, 1:2])).then_inc(lam_step, 1)
            act.wait_ge(gw_ld, 16)
            nc.scalar.activation(GWH[:, :, :], GWR[:, :, :], ACT.Copy).then_inc(gw_hi, 1)

            def gates(n):
                if n >= 2:
                    act.wait_ge(scan_done, n - 1)
                for c in range(3):
                    act.wait_ge(gate_mm, 3 * n + c + 1)
                    for bank, out, bias in ((6, GR, 5), (7, GI, 6)):
                        nc.scalar.activation(out[:, n % 2, c * CH:(c + 1) * CH], psum[:, bank, 0:CH],
                                             ACT.Sigmoid, bias=apar[:, n, bias:bias + 1]).then_inc(gate_rd, 1)

            def decay(n):
                act.wait_ge(gate_rd, 6 * (n + 1))
                act.wait_ge(lam_step, 5)
                nc.scalar.activation(TM[:, n % 2, :], GR[:, n % 2, :], ACT.Tanh,
                                     scale=clam[:, n, 1:2]).then_inc(tanh_done, 1)
                nc.scalar.activation(GR[:, n % 2, :], GR[:, n % 2, :], ACT.Exp,
                                     scale=clam[:, n, 0:1]).then_inc(a0_done, 1)

            def coefficients(n):
                act.wait_ge(mm2_done, n + 1)
                nc.scalar.activation(GR[:, n % 2, :], GR[:, n % 2, :], ACT.Sqrt,
                                     scale=-1.0).then_inc(root_done, 1)

            def y_split_hi(n):
                act.wait_ge(y_done, n + 1)
                nc.scalar.activation(YH[:, n, :], U[:, n % 2, :], ACT.Copy).then_inc(y_hi, 1)

            for w in range(1, J_F0 + 1):
                hi_weights(act, w + 1)
                if 0 <= w - 9 < KT:
                    act.wait_ge(acc_read, w)
                    nc.scalar.activation(U[:, (w - 9) % 2, :], U[:, (w - 9) % 2, :],
                                         ACT.Gelu_apprx_tanh).then_inc(br_gelu, 1)
                if 0 <= w - 2 < KT:
                    gates(w - 2)
                if w - 1 < KT:
                    n = w - 1
                    act.wait_ge(xc_done, 2 * (n + 1))
                    wait(act, gate_mm, 3 * n)
                    nc.scalar.activation(XCH[:, :], XC[:, n % 2, 0:T], ACT.Copy).then_inc(xc_hi, 1)
                if 0 <= w - 3 < KT:
                    coefficients(w - 3)
                if 0 <= w - 2 < KT:
                    decay(w - 2)
                if 0 <= w - 10 < KT - 1:
                    y_split_hi(w - 10)
                if w == 16:
                    y_split_hi(KT - 1)
                if w > J_AOUT:
                    d = w - 1 - J_AOUT
                    split_hi(act, 1, d, acc_read, J_AOUT + d + 1, gain=1)
            root(act, 1)

            def conv_rows(f):
                nc.scalar.activation(windows(GB[:, :], WF - 1 + SEQ, DS + WF - 1)[:, :, 0:WF - 1],
                                     fst[:, f, :, :], ACT.Copy).then_inc(f_win, 1)

            def ffn(L, step, last):
                first = (J_F0, J_F1)[L]
                act.wait_ge(f_par, 32 * (L * FSTEPS + step + 1))
                conv_rows(0)
                for j in range(FJ):
                    f = j // 2
                    F = L * FSTEPS * FT + f + FT * step
                    hi_weights(act, first + j + 2, FJ, step)
                    if j < 2 * FT and j % 2 == 0:
                        act.wait_ge(f_c3, 2 * F + 2)
                        nc.scalar.activation(CB[:, f % 2, 0:T], CB[:, f % 2, 0:T],
                                             ACT.Gelu_apprx_tanh).then_inc(f_gelu, 1)
                        if f == 0:
                            wait(act, f_out, 32 * (L * FSTEPS + step))
                        nc.scalar.activation(fop[:, f, :], GB[:, SEQ:SEQ + WF - 1], ACT.Copy).then_inc(f_rows, 1)
                        nc.scalar.activation(fos[:, f, :, :],
                                             windows(GB[:, :], WF - 1 + SEQ, DS + WF - 1)[:, :, DS:],
                                             ACT.Copy).then_inc(f_rows, 1)
                        if f + 1 < FT:
                            conv_rows(f + 1)
                    elif j < 2 * FT:
                        act.wait_ge(h_done, F + 1)
                        nc.scalar.activation(FYH[:, f, :], U[:, f % 2, :], ACT.Copy).then_inc(h_hi, 1)
                    elif last:
                        d = j - 2 * FT
                        split_hi(act, 2 + 2 * L, d, acc_read, first + j + 1 + FJ * step, split=(L == 0))
                        if L == 1:
                            act.wait_ge(sq_done, KT * 4 + d + 1)
                            nc.scalar.activation(X[:, d, :], X[:, d, :], ACT.Copy,
                                                 scale=gains[:, 5, d:d + 1]).then_inc(y_gained, 1)

            def ffn_layer(L):
                act.wait_ge(job_done, (J_F0, J_F1)[L])
                ffn(L, 0, False)
                with act.Fori(1, FSTEPS - 1) as step:
                    ffn(L, step, False)
                ffn(L, FSTEPS - 1, True)

            ffn_layer(0)
            root(act, 2)
            hi_weights(act, J_FG + 2)
            act.wait_ge(fg_step, 2)
            nc.scalar.activation(VS[0:NH, :], VS[0:NH, :], ACT.Exp).then_inc(fg_act, 1)
            act.wait_ge(fg_act, 1)
            nc.scalar.activation(VS[0:NH, :], VS[0:NH, :], ACT.Ln, bias=cvec[0:NH, 1:2]).then_inc(fg_act, 1)
            hi_weights(act, J_FG + 3)
            hi_weights(act, J_FG + 4)

            def pair(c, t):
                hp, u0 = c + 2 * t, UNITS * c + 2 * UNITS * t

                def jq(r):
                    return J_QKV + 3 * c + r, 6, t

                wait(act, qk_done, u0)
                act.wait_ge(acc_read, J_QKV + 3 * c + 2 + 6 * t)
                nc.scalar.activation(QH[:, :], QS[:, 0:SEQ], ACT.Copy).then_inc(q_hi, 1)
                nc.scalar.activation(KH[:, :], KS[:, 0:SEQ], ACT.Copy).then_inc(k_hi, 1)
                wait(act, pv_done, u0)
                act.wait_ge(v_t, 1 + 2 * c + 4 * t)
                nc.scalar.activation(VH[:, :, :].rearrange("p a b -> p (a b)"), T_ps[:, 0:SEQ],
                                     ACT.Copy).then_inc(v_hi, 1)
                act.wait_ge(v_t, 2 + 2 * c + 4 * t)
                nc.scalar.activation(VN[:, :], O_ps[0:NS, 0:P], ACT.Copy).then_inc(vn_rd, 1)
                for v in range(UNITS + 2):
                    if v < UNITS:
                        rows, n = (2 * NS, DK) if v == 0 else (P, P * (UNIT_OF[v][1] + 1))
                        act.wait_ge(s_read, u0 + v + 1)
                        nc.scalar.activation(SB[0:rows, v % 2, 0:n], SB[0:rows, v % 2, 0:n], ACT.Exp,
                                             bias=nmax[0:rows, v:v + 1], scale=-1.0,
                                             accum_out=lsum[0:rows, v:v + 1]).then_inc(e_done, 1)
                    if v == 1:
                        act.wait_ge(t_done, u0 + v)
                        nc.scalar.activation(PTD[:, 0:4 * NS], T_ps[:, 0:4 * NS], ACT.Copy)
                        nc.scalar.activation(PTD[0:NS, 4 * NS:6 * NS], T_ps[0:NS, 4 * NS:6 * NS],
                                             ACT.Copy).then_inc(pt_hi, 1)
                    elif 2 <= v <= UNITS:
                        n = P * (UNIT_OF[v - 1][1] + 1)
                        act.wait_ge(t_done, u0 + v)
                        act.wait_ge(pv_done, u0 + max(v - 2, 1))
                        nc.scalar.activation(PTH[:, (v - 1) % 2, 0:n], T_ps[:, 0:n],
                                             ACT.Copy).then_inc(pt_hi, 1)
                    if v >= 2:
                        act.wait_ge(pv_done, u0 + v - 1)
                        if v == 2:
                            for h in range(2):
                                rows = slice(HD * h, HD * (h + 1))
                                o_d = O_ps[rows, 0:2 * NS].rearrange("p (b h j) -> p b h j", h=2, j=DS)
                                last_ = nc.scalar.activation(
                                    X[rows, hp, SEQ:T].rearrange("p (b j) -> p b j", j=DS),
                                    o_d[:, :, h, :], ACT.Copy)
                            last_.then_inc(o_read, 1)
                        else:
                            h, i = UNIT_OF[v - 2]
                            nc.scalar.activation(X[HD * h:HD * (h + 1), hp, P * i:P * (i + 1)],
                                                 O_ps[0:HD, 0:P], ACT.Copy).then_inc(o_read, 1)
                    if v in SPLIT_SLOTS and c < NHP - 1:
                        hi_weights(act, *jq(4 + SPLIT_SLOTS.index(v)))

            over_pairs(act, pair)
            hi_weights(act, J_O + 1)
            act.wait_ge(k_out, 16 * NHP)
            act.wait_ge(v_out, 16 * NHP)
            act.wait_ge(o_read, UNITS * NHP)
            for d in range(KT):
                nc.scalar.activation(YH[:, d, :], X[:, d, :], ACT.Copy).then_inc(o_hi, 1)
            for d in range(KT):
                hi_weights(act, J_O + d + 2)
                split_hi(act, 3, d, res_done, d + 1, gain=4)
            root(act, 3)
            ffn_layer(1)
            root(act, 4)

        @block.tensor
        def _(pe):
            def stream_ready(p):
                return lambda k: pe.wait_ge(x_lo, KT * p + k + 1)

            def gate_chunk(n, c):
                if c == 0:
                    pe.wait_ge(xc_lo, n + 1)
                    if n == 0:
                        pe.wait_ge(gw_lo, 1)
                        pe.wait_ge(sqrt_done, 3)
                wait(pe, gate_rd, 2 * (3 * n + c))
                cols = slice(c * CH, (c + 1) * CH)
                for g in range(2):
                    wh, wl = GWH[:, n, g * P:(g + 1) * P], GWL[:, n, g * P:(g + 1) * P]
                    nc.tensor.matmul(psum[:, 6 + g, 0:CH], wh, XCH[:, cols], start=True, stop=False)
                    nc.tensor.matmul(psum[:, 6 + g, 0:CH], wh, XCL[:, cols], start=False, stop=False)
                    mm = nc.tensor.matmul(psum[:, 6 + g, 0:CH], wl, XCH[:, cols], start=False, stop=True)
                mm.then_inc(gate_mm, 1)

            for J in range(J_F0):
                if J < J_AOUT:
                    n = J - 2
                    job(pe, J, 0, 0, XH, XL, before_k=stream_ready(0) if J == 0 else None,
                        after_k=(lambda k: gate_chunk(n, k - 2) if k in (2, 3, 4) else None) if 0 <= n < KT else None)
                    if J == 0:
                        pe.wait_ge(ones_ld, 32)
                        mean_square(pe, 0)
                else:
                    job(pe, J, 0, 0, YH, YL,
                        before_k=(lambda k: pe.wait_ge(y_lo, k + 1)) if J == J_AOUT else None)

            def ffn(L, step, head=False):
                first = (J_F0, J_F1)[L]
                for j in range(2 * FT):
                    job(pe, first + j, FJ, step, XH, XL,
                        before_k=stream_ready(1 + 2 * L) if head and j == 0 else None)
                    if head and j == 0:
                        mean_square(pe, 1 + 2 * L)
                for d in range(KT):
                    hidden = (lambda k: pe.wait_ge(h_lo, L * FSTEPS * FT + k + 1 + FT * step)) if d == 0 else None
                    job(pe, first + 2 * FT + d, FJ, step, FYH, FYL, nk=FT, before_k=hidden)

            def ffn_layer(L):
                ffn(L, 0, head=True)
                with pe.Fori(1, FSTEPS - 1) as step:
                    ffn(L, step)
                ffn(L, FSTEPS - 1)

            ffn_layer(0)
            job(pe, J_FG, 0, 0, XH, XL, before_k=stream_ready(2), m=NH)
            mean_square(pe, 2)
            job(pe, J_QKV, 0, 0, XH, XL)
            job(pe, J_QKV + 1, 0, 0, XH, XL)
            pe.wait_ge(lf_ready, 1)
            pe.wait_ge(sqrt_done, 9)
            nc.tensor.transpose(O_ps[0:NS, 0:NH], VS[0:NH, SEQ:T], ident[0:NH, 0:NH]).then_inc(lnt, 1)
            job(pe, J_QKV + 2, 0, 0, XH, XL)
            pe.wait_ge(acc_read, J_QKV + 3)
            pe.wait_ge(b_const, 16 * B_CONSTS)
            pe.wait_ge(lnx, 1)
            nc.tensor.matmul(S_ps[:, 0:DK], LP[:, 0, :, :].rearrange("p b h -> p (b h)"), C0[:, :],
                             start=True, stop=False)
            nc.tensor.matmul(S_ps[:, 0:DK], LP[:, 1, :, :].rearrange("p b h -> p (b h)"), C1[:, :],
                             start=False, stop=False)
            nc.tensor.matmul(S_ps[:, 0:DK], LNX[:, :, :].rearrange("p b h -> p (b h)"), CN[:, :],
                             start=False, stop=True).then_inc(df_mm, 1)

            def pair(c, t):
                u0, last = UNITS * c + 2 * UNITS * t, c == NHP - 1
                steps = [] if last else [(r, k) for r in range(3) for k in range(KT)]

                def project():
                    if not steps:
                        return
                    r, k = steps.pop(0)
                    first = J_QKV + 3 * (c + 1) + r
                    if k == 0:
                        pe.wait_ge(w_ready, first + 1 + 6 * t)
                        pe.wait_ge(acc_read, first + 6 * t)
                    mm = k_step(k, 0, first % 2, XH, XL, KT)
                    if k == KT - 1:
                        mm.then_inc(job_done, 1)

                def values():
                    pe.wait_ge(acc_read, J_QKV + 3 * c + 3 + 6 * t)
                    wait(pe, pt_lo, (UNITS - 1) * (c + 2 * t))
                    wait(pe, o_read, u0)
                    for kb in range(NQB):
                        mm = nc.tensor.transpose(T_ps[:, P * kb:P * (kb + 1)], VS[:, P * kb:P * (kb + 1)],
                                                 ident[:, :])
                    mm.then_inc(v_t, 1)
                    nc.tensor.transpose(O_ps[0:NS, 0:P], VS[:, SEQ:T], ident[:, :]).then_inc(v_t, 1)

                def logits(v):
                    if v > 0 or c > 0:
                        pe.wait_ge(s_read, u0 + v)
                    if v == 0:
                        pe.wait_ge(df_rd, 1)
                        pe.wait_ge(sel_ld, 16 * (c + 1) + 32 * t)
                        pe.wait_ge(qd_done, 4 * (c + 1) + 8 * t)
                        nc.tensor.matmul(S_ps[0:2 * NS, 0:DK], SEL[:, :], DFc[:, :], start=True, stop=False,
                                         skip_group_check=True)
                        for b in range(DB):
                            pe.wait_ge(cc_ld[b], 32 * (2 * c + 1) + 128 * t)
                            nc.tensor.matmul(S_ps[0:2 * NS, 0:PAST], QX[:, b, :], CC[:, b, :],
                                             start=False, stop=False, skip_group_check=True)
                        nc.tensor.matmul(S_ps[0:2 * NS, PAST:DK], QD[:, :, :, :].rearrange("p b h j -> p (b h j)"),
                                         KS[:, SEQ:T], start=False, stop=True,
                                         skip_group_check=True).then_inc(qk_done, 1)
                        return
                    if v == 1:
                        pe.wait_ge(mask_ready, 2)
                        pe.wait_ge(q_lo, c + 1 + 2 * t)
                        pe.wait_ge(k_lo, c + 1 + 2 * t)
                    h, i = UNIT_OF[v]
                    rows, q, n = slice(HD * h, HD * (h + 1)), slice(P * i, P * (i + 1)), P * (i + 1)
                    for a in range(0, n, 512):
                        b = min(a + 512, n)
                        for x, y, part in ((QH, KH, 0), (QH, KL, 1), (QL, KH, 2)):
                            nc.tensor.matmul(S_ps[:, a:b], x[rows, q], y[rows, a:b], start=(part == 0),
                                             stop=False, skip_group_check=True)
                    nc.tensor.matmul(S_ps[:, n - P:n], identB[:, :], maskB[:, :], start=False, stop=True,
                                     skip_group_check=True).then_inc(qk_done, 1)

                def turn(v):
                    if v == 0:
                        pe.wait_ge(v_lo, c + 1 + 2 * t)
                        wait_apart(pe, p_norm, u0 + v + 1, probs_seen)
                        for g in range(2):
                            nc.tensor.transpose(T_ps[:, 2 * NS * g:2 * NS * (g + 1)],
                                                SB[0:2 * NS, 0, PAGE * g:PAGE * (g + 1)],
                                                ident[0:2 * NS, 0:2 * NS])
                        nc.tensor.transpose(T_ps[0:NS, 4 * NS:6 * NS], SB[0:2 * NS, 0, PAST:DK],
                                            ident[0:2 * NS, 0:2 * NS]).then_inc(t_done, 1)
                        return
                    if v == 1:
                        pe.wait_ge(pt_hi, u0 + 1)
                    else:
                        pe.wait_ge(pt_lo, (UNITS - 1) * c + v - 1 + 2 * (UNITS - 1) * t)
                    pe.wait_ge(p_norm, u0 + v + 1)
                    for kb in range(UNIT_OF[v][1] + 1):
                        mm = nc.tensor.transpose(T_ps[:, P * kb:P * (kb + 1)],
                                                 SB[:, v % 2, P * kb:P * (kb + 1)], ident[:, :])
                    mm.then_inc(t_done, 1)

                def product(v):
                    if v == 0:
                        pe.wait_ge(pt_hi, u0 + 1)
                        pe.wait_ge(vn_rd, c + 1 + 2 * t)
                        nc.tensor.matmul(O_ps[:, 0:2 * NS], VN[:, :], PTD[0:NS, 4 * NS:6 * NS],
                                         start=True, stop=False, skip_group_check=True)
                        for b in range(DB):
                            pe.wait_ge(cc_ld[b], 32 * (2 * c + 2) + 128 * t)
                            for g in range(NPG):
                                cols = slice(2 * NS * g + 2 * DS * b, 2 * NS * g + 2 * DS * (b + 1))
                                mm = nc.tensor.matmul(O_ps[:, 2 * DS * b:2 * DS * (b + 1)],
                                                      CC[:, b, PAGE * g:PAGE * (g + 1)], PTD[:, cols],
                                                      start=False, stop=(b == DB - 1 and g == NPG - 1),
                                                      skip_group_check=True)
                        mm.then_inc(pv_done, 1)
                        return
                    h, i = UNIT_OF[v]
                    pe.wait_ge(pt_lo, (UNITS - 1) * c + v + 2 * (UNITS - 1) * t)
                    pe.wait_ge(o_read, u0 + v)
                    cols = slice(HD * h, HD * (h + 1))
                    for kb in range(i + 1):
                        keys = slice(P * kb, P * (kb + 1))
                        for x, y, part in ((VH, PTH, 0), (VH, PTL, 1), (VL, PTH, 2)):
                            mm = nc.tensor.matmul(O_ps[0:HD, 0:P], x[:, kb, cols], y[:, v % 2, keys],
                                                  start=(kb == 0 and part == 0), stop=(kb == i and part == 2))
                    mm.then_inc(pv_done, 1)

                values()
                for v in range(UNITS + 2):
                    if v == 0:
                        for _ in range(KSTEPS[0]):
                            project()
                    if v < UNITS:
                        logits(v)
                    if v > 0:
                        for _ in range(KSTEPS[v]):
                            project()
                    if 1 <= v <= UNITS:
                        turn(v - 1)
                    if v >= 2:
                        product(v - 2)

            over_pairs(pe, pair)
            for d in range(KT):
                job(pe, J_O + d, 0, 0, YH, YL, before_k=(lambda k: pe.wait_ge(o_lo, k + 1)) if d == 0 else None)
            ffn_layer(1)
            mean_square(pe, 4)

        @block.vector
        def _(dve):
            for d in range(KT):
                split_lo(dve, 0, d, gain=0)
                if d == 0:
                    lo_weights(dve, 0)
            lo_weights(dve, 1)
            dve.wait_ge(const_ld, 80)
            nc.vector.scalar_tensor_tensor(clam[:, :, 0], apar[:, :, 7], -1.0, apar[:, :, 7],
                                           ALU.mult, ALU.min).then_inc(lam_step, 1)
            inverse(dve, 0)
            dve.wait_ge(lam_step, 3)
            nc.vector.scalar_tensor_tensor(clam[:, :, 1], apar[:, :, 7], 0.0, clam[:, :, 0],
                                           ALU.min, ALU.subtract).then_inc(lam_step, 1)
            dve.wait_ge(lam_step, 4)
            nc.vector.tensor_scalar(clam[:, :, 0], clam[:, :, 1], 8.0, None, ALU.mult)
            nc.vector.tensor_scalar(clam[:, :, 1], clam[:, :, 1], -4.0, None, ALU.mult).then_inc(lam_step, 1)
            dve.wait_ge(gw_hi, 1)
            nc.vector.tensor_tensor(GWL[:, :, :], GWR[:, :, :], GWH[:, :, :].bitcast(F32),
                                    ALU.subtract).then_inc(gw_lo, 1)

            def tail_b(n):
                dve.wait_ge(b_done, 2 * (n + 1))
                dve.wait_ge(a_done, 2 * (n + 1))
                nc.vector.tensor_tensor_scan(X[:, n, 0:SEQ], TM[:, n % 2, 0:SEQ], GI[:, n % 2, 0:SEQ], 0.0,
                                             ALU.mult, ALU.add).then_inc(scan_done, 1)

            def branch_y(n):
                dve.wait_ge(br_gelu, n + 1)
                nc.vector.tensor_tensor(U[:, n % 2, :], U[:, n % 2, :], X[:, n, :], ALU.mult).then_inc(y_done, 1)

            def branch_lo(n):
                dve.wait_ge(y_hi, n + 1)
                nc.vector.tensor_tensor(YL[:, n, :], U[:, n % 2, :], YH[:, n, :].bitcast(F32),
                                        ALU.subtract).then_inc(y_lo, 1)

            for w in range(1, J_F0 + 1):
                J, n3 = w - 1, w - 3
                if 0 <= n3 < KT:
                    dve.wait_ge(tanh_done, n3 + 1)
                    dve.wait_ge(a0_done, n3 + 1)
                    nc.vector.scalar_tensor_tensor(TM[:, n3 % 2, :], GR[:, n3 % 2, :], 1.0, TM[:, n3 % 2, :],
                                                   ALU.add, ALU.mult).then_inc(m_done, 1)
                dve.wait_ge(job_done, J + 1)
                if J < J_BR:
                    if J >= 2:
                        dve.wait_ge(a_rows, 2 * (J - 1))
                    scaled_in(dve, J % 2, RB[:, J % 2, :], WA - 1, DS + WA - 1).then_inc(acc_read, 1)
                elif J < J_AOUT:
                    n = J - J_BR
                    wait(dve, y_lo, n - 1)
                    scaled(dve, J % 2, U[:, n % 2, :]).then_inc(acc_read, 1)
                else:
                    d = J - J_AOUT
                    dve.wait_ge(x_ld[d], 32)
                    nc.vector.tensor_tensor(thirds(X[:, d, :]), acc(J % 2), thirds(X[:, d, :]),
                                            ALU.add).then_inc(acc_read, 1)
                lo_weights(dve, J + 2)
                if 0 <= n3 < KT:
                    dve.wait_ge(m_done, n3 + 1)
                    nc.vector.scalar_tensor_tensor(GR[:, n3 % 2, :], TM[:, n3 % 2, :], 2.0, TM[:, n3 % 2, :],
                                                   ALU.subtract, ALU.mult).then_inc(mm2_done, 1)
                if J < J_BR:
                    b = J % 2
                    if J == 0:
                        dve.wait_ge(a_pad, 2)
                    if J >= 2:
                        dve.wait_ge(ix_done, J - 1)
                    dve.wait_ge(a_win, J + 1)
                    dve.wait_ge(acc_read, J + 1)
                    nc.vector.tensor_scalar(XC[:, b, 0:CW], RB[:, b, 3:RW], apar[:, J, 3:4], apar[:, J, 4:5],
                                            ALU.mult, ALU.add).then_inc(a_conv, 1)
                    for s in (2, 1):
                        dve.wait_ge(a_conv, 3 * J + 3 - s)
                        nc.vector.scalar_tensor_tensor(XC[:, b, 0:CW], RB[:, b, s:s + CW], apar[:, J, s:s + 1],
                                                       XC[:, b, 0:CW], ALU.mult, ALU.add).then_inc(a_conv, 1)
                    dve.wait_ge(a_conv, 3 * J + 3)
                    nc.vector.scalar_tensor_tensor(XC[:, b, 0:SEQ], RB[:, b, 0:SEQ], apar[:, J, 0:1],
                                                   XC[:, b, 0:SEQ], ALU.mult, ALU.add).then_inc(xc_done, 1)
                    nc.vector.scalar_tensor_tensor(
                        XC[:, b, SEQ:T].rearrange("p (b r) -> p b r", r=DS),
                        windows(RB[:, b, :], SEQ + 3, DS + 3)[:, :, 0:DS], apar[:, J, 0:1],
                        windows(XC[:, b, :], SEQ + 3, DS + 3)[:, :, 0:DS],
                        ALU.mult, ALU.add).then_inc(xc_done, 1)
                if J < J_BR:
                    dve.wait_ge(xc_hi, J + 1)
                    nc.vector.tensor_tensor(XCL[:, :], XC[:, J % 2, 0:T], XCH[:, :].bitcast(F32),
                                            ALU.subtract).then_inc(xc_lo, 1)
                if 0 <= n3 < KT:
                    tail_b(n3)
                if w == 10:
                    dve.wait_ge(b_done, 2 * KT)
                    dve.wait_ge(a_done, 2 * KT)
                    nc.vector.tensor_tensor_scan(hS[:, :, :, :].rearrange("p n b r -> p (n b r)"),
                                                 aS[:, :, :, :].rearrange("p n b r -> p (n b r)"),
                                                 bS[:, :, :, :].rearrange("p n b r -> p (n b r)"), 0.0,
                                                 ALU.mult, ALU.add).then_inc(hs_done, 1)
                    dve.wait_ge(hs_done, 1)
                    dve.wait_ge(scan_done, KT)
                    nc.vector.tensor_copy(X[:, :, SEQ:T].rearrange("p n (b r) -> p n b r", r=DS),
                                          hS[:, :, :, 1:]).then_inc(h_dec, 1)
                    nc.vector.tensor_copy(hl[:, :, 0], X[:, :, SEQ - 1]).then_inc(h_dec, 1)
                    nc.vector.tensor_copy(hl[:, :, 1:], hS[:, :, :, DS]).then_inc(h_dec, 1)
                    dve.wait_ge(h_dec, 3)
                if 0 <= w - 10 < KT - 1:
                    branch_y(w - 10)
                    if w == 16:
                        branch_y(KT - 1)
                    branch_lo(w - 10)
                    if w == 16:
                        branch_lo(KT - 1)
                if w > J_AOUT:
                    split_lo(dve, 1, J - J_AOUT, gain=1)
            inverse(dve, 1)

            def ffn(L, step, last):
                first = (J_F0, J_F1)[L]

                def hidden_lo(f):
                    dve.wait_ge(h_hi, L * FSTEPS * FT + f + 1 + FT * step)
                    nc.vector.tensor_tensor(FYL[:, f, :], U[:, f % 2, :], FYH[:, f, :].bitcast(F32),
                                            ALU.subtract).then_inc(h_lo, 1)

                for j in range(FJ):
                    J, slot, f = first + j + FJ * step, (first + j) % 2, j // 2
                    F = L * FSTEPS * FT + f + FT * step
                    dve.wait_ge(job_done, J + 1)
                    if j < 2 * FT and j % 2 == 0:
                        wait(dve, f_rows, 2 * F)
                        scaled_in(dve, slot, GB, WF - 1, DS + WF - 1).then_inc(acc_read, 1)
                        if f > 0:
                            hidden_lo(f - 1)
                        lo_weights(dve, first + j + 2, FJ, step)
                        c = f % 2
                        dve.wait_ge(f_pad, L + 1)
                        dve.wait_ge(f_win, F + 1)
                        dve.wait_ge(acc_read, J + 1)
                        nc.vector.tensor_scalar(CB[:, c, 0:FW], GB[:, 2:GW], fpar[:, f, 2:3], fpar[:, f, 3:4],
                                                ALU.mult, ALU.add).then_inc(f_c1, 1)
                        dve.wait_ge(f_c1, F + 1)
                        nc.vector.scalar_tensor_tensor(CB[:, c, 0:FW], GB[:, 1:1 + FW], fpar[:, f, 1:2],
                                                       CB[:, c, 0:FW], ALU.mult, ALU.add).then_inc(f_c2, 1)
                        dve.wait_ge(f_c2, F + 1)
                        nc.vector.scalar_tensor_tensor(CB[:, c, 0:SEQ], GB[:, 0:SEQ], fpar[:, f, 0:1],
                                                       CB[:, c, 0:SEQ], ALU.mult, ALU.add).then_inc(f_c3, 1)
                        nc.vector.scalar_tensor_tensor(
                            CB[:, c, SEQ:T].rearrange("p (b r) -> p b r", r=DS),
                            windows(GB[:, :], SEQ + 2, DS + 2)[:, :, 0:DS], fpar[:, f, 0:1],
                            windows(CB[:, c, :], SEQ + 2, DS + 2)[:, :, 0:DS],
                            ALU.mult, ALU.add).then_inc(f_c3, 1)
                    elif j < 2 * FT:
                        wait(dve, h_lo, F - 1)
                        scaled(dve, slot, U[:, f % 2, :]).then_inc(acc_read, 1)
                        lo_weights(dve, first + j + 2, FJ, step)
                        dve.wait_ge(f_gelu, F + 1)
                        dve.wait_ge(acc_read, J + 1)
                        nc.vector.tensor_tensor(U[:, f % 2, :], U[:, f % 2, :], CB[:, f % 2, 0:T],
                                                ALU.mult).then_inc(h_done, 1)
                        if f == FT - 1:
                            hidden_lo(f)
                    else:
                        d = j - 2 * FT
                        nc.vector.tensor_tensor(thirds(X[:, d, :]), acc(slot), thirds(X[:, d, :]),
                                                ALU.add).then_inc(acc_read, 1)
                        lo_weights(dve, first + j + 2, FJ, step)
                        if last and L == 0:
                            split_lo(dve, 2, d)

            def ffn_layer(L):
                ffn(L, 0, False)
                with dve.Fori(1, FSTEPS - 1) as step:
                    ffn(L, step, False)
                ffn(L, FSTEPS - 1, True)

            ffn_layer(0)
            inverse(dve, 2)
            lo_weights(dve, J_FG + 2)
            dve.wait_ge(job_done, J_FG + 1)
            zf, lf = KS[0:NH, :], VS[0:NH, :]
            nc.vector.tensor_tensor(thirds(zf), psum[0:NH, 0:3, 0:CH], thirds(RS[0:NH, :]),
                                    ALU.mult).then_inc(acc_read, 1)
            dve.wait_ge(acc_read, J_FG + 1)
            dve.wait_ge(b_const, 16 * B_CONSTS)
            nc.vector.tensor_scalar(zf, zf, bfg[:, 0:1], None, ALU.add).then_inc(fg_step, 1)
            dve.wait_ge(fg_step, 1)
            nc.vector.scalar_tensor_tensor(lf, zf, -1.0, zf, ALU.mult, ALU.min).then_inc(fg_step, 1)
            dve.wait_ge(fg_act, 2)
            nc.vector.scalar_tensor_tensor(lf, zf, 0.0, lf, ALU.min, ALU.subtract).then_inc(lf_ready, 1)
            dve.wait_ge(lf_ready, 1)
            dve.wait_ge(fg_one, 1)
            nc.vector.tensor_tensor_scan(KS[0:NH, 0:SEQ], ON16[:, :], lf[:, 0:SEQ], 0.0,
                                         ALU.mult, ALU.add).then_inc(fg_step, 1)
            dve.wait_ge(fg_step, 3)
            nc.vector.tensor_scalar(KS[0:NH, 0:SEQ], KS[0:NH, 0:SEQ], -1.0 / SCALE, None,
                                    ALU.mult).then_inc(fg_step, 1)
            dve.wait_ge(job_done, J_QKV + 1)
            scaled(dve, J_QKV % 2, QS[:, :]).then_inc(acc_read, 1)
            lo_weights(dve, J_FG + 3)
            nc.vector.memset(QXd[:, :, :], 0.0).then_inc(qx_zero, 1)
            nc.vector.memset(QD[:, :, :, :], 0.0).then_inc(qx_zero, 1)
            dve.wait_ge(job_done, J_QKV + 2)
            dve.wait_ge(nf_out, 16)
            scaled(dve, (J_QKV + 1) % 2, KS[:, :]).then_inc(acc_read, 1)
            lo_weights(dve, J_FG + 4)
            dve.wait_ge(lnt, 1)
            nc.vector.tensor_copy(LNX[:, :, :], O_ps[0:NS, 0:NH].unsqueeze(1).to_broadcast([NS, DB, NH])
                                  ).then_inc(lnx, 1)

            def v_in(c, t):
                dve.wait_ge(job_done, J_QKV + 3 * c + 3 + 6 * t)
                wait(dve, v_t, 2 * c + 4 * t)
                wait(dve, v_out, 16 * c + 32 * t)
                scaled(dve, (J_QKV + 2) % 2 if c == 0 else 0, VS[:, :]).then_inc(acc_read, 1)

            dve.wait_ge(lf_out, 16)
            v_in(0, 0)
            dve.wait_ge(df_mm, 1)
            nc.vector.tensor_copy(DFc[:, :], S_ps[:, 0:DK]).then_inc(df_rd, 1)
            dve.wait_ge(qx_zero, 2)
            dve.wait_ge(f_out, 32 * FSTEPS)

            def pair(c, t):
                hp, u0 = c + 2 * t, UNITS * c + 2 * UNITS * t
                if c > 0:
                    v_in(c, t)
                dve.wait_ge(q_hi, c + 1 + 2 * t)
                nc.vector.tensor_tensor(QL[:, :], QS[:, 0:SEQ], QH[:, :].bitcast(F32), ALU.subtract
                                        ).then_inc(q_lo, 1)
                for h in range(2):
                    rows = slice(HD * h, HD * (h + 1))
                    q = QS[rows, SEQ:T].rearrange("p (b j) -> p b j", j=DS)
                    nc.vector.tensor_copy(QXd[rows, :, DS * h:DS * (h + 1)], q).then_inc(qd_done, 1)
                    nc.vector.tensor_copy(QD[rows, :, h, :], q).then_inc(qd_done, 1)
                dve.wait_ge(k_hi, c + 1 + 2 * t)
                nc.vector.tensor_tensor(KL[:, :], KS[:, 0:SEQ], KH[:, :].bitcast(F32), ALU.subtract
                                        ).then_inc(k_lo, 1)
                dve.wait_ge(v_hi, c + 1 + 2 * t)
                nc.vector.tensor_tensor(VL[:, :, :].rearrange("p a b -> p (a b)"), T_ps[:, 0:SEQ],
                                        VH[:, :, :].rearrange("p a b -> p (a b)").bitcast(F32), ALU.subtract
                                        ).then_inc(v_lo, 1)
                for v in range(UNITS + 1):
                    if v < UNITS:
                        rows, n = (2 * NS, DK) if v == 0 else (P, P * (UNIT_OF[v][1] + 1))
                        wait(dve, t_done, u0 + max(v - 1, 0))
                        if v in (1, 1 + NQB):
                            dve.wait_ge(nf_ld, 16 * (2 * c + 1 + (v > 1)) + 64 * t)
                        wait_apart(dve, qk_done, u0 + v + 1, logits_seen)
                        nc.vector.tensor_tensor_reduce(
                            SB[0:rows, v % 2, 0:n], S_ps[0:rows, 0:n], DM[:, :] if v == 0 else NF[:, 0:n],
                            -SCALE, 3.0e38, ALU.add, ALU.min, nmax[0:rows, v:v + 1]).then_inc(s_read, 1)
                    if v - 1 in SPLIT_SLOTS and c < NHP - 1:
                        lo_weights(dve, J_QKV + 3 * c + 4 + SPLIT_SLOTS.index(v - 1), 6, t)
                    if v == 5 and c < NHP - 1:
                        dve.wait_ge(job_done, J_QKV + 3 * c + 4 + 6 * t)
                        scaled(dve, 0, QS[:, :]).then_inc(acc_read, 1)
                    if v == 13 and c < NHP - 1:
                        dve.wait_ge(job_done, J_QKV + 3 * c + 5 + 6 * t)
                        dve.wait_ge(k_out, 16 * (c + 1) + 32 * t)
                        scaled(dve, 0, KS[:, :]).then_inc(acc_read, 1)
                    if v < UNITS:
                        dve.wait_ge(e_done, u0 + v + 1)
                        nc.vector.reciprocal(linv[0:rows, v:v + 1], lsum[0:rows, v:v + 1]).then_inc(rl_done, 1)
                        dve.wait_ge(rl_done, u0 + v + 1)
                        nc.vector.tensor_scalar(SB[0:rows, v % 2, 0:n], SB[0:rows, v % 2, 0:n],
                                                linv[0:rows, v:v + 1], None, ALU.mult).then_inc(p_norm, 1)
                    if v >= 2:
                        m = P * (UNIT_OF[v - 1][1] + 1)
                        dve.wait_ge(pt_hi, u0 + v)
                        dve.wait_ge(pv_done, u0 + max(v - 2, 1))
                        nc.vector.tensor_tensor(PTL[:, (v - 1) % 2, 0:m], T_ps[:, 0:m],
                                                PTH[:, (v - 1) % 2, 0:m].bitcast(F32), ALU.subtract
                                                ).then_inc(pt_lo, 1)

            over_pairs(dve, pair)
            lo_weights(dve, J_O + 1)
            for d in range(KT):
                dve.wait_ge(o_hi, d + 1)
                nc.vector.tensor_tensor(YL[:, d, :], X[:, d, :], YH[:, d, :].bitcast(F32),
                                        ALU.subtract).then_inc(o_lo, 1)
            for d in range(KT):
                dve.wait_ge(job_done, J_O + d + 1)
                nc.vector.tensor_tensor(thirds(X[:, d, :]), acc((J_O + d) % 2), thirds(XH[:, d, :].bitcast(F32)),
                                        ALU.add).then_inc(acc_read, 1)
                lo_weights(dve, J_O + d + 2)
                dve.wait_ge(acc_read, J_O + d + 1)
                nc.vector.tensor_tensor(X[:, d, :], X[:, d, :], XL[:, d, :].bitcast(F32),
                                        ALU.add).then_inc(res_done, 1)
                if d > 0:
                    split_lo(dve, 3, d - 1, gain=4)
            split_lo(dve, 3, KT - 1, gain=4)
            inverse(dve, 3)
            ffn_layer(1)
            inverse(dve, 4)
            for d in range(POOL_TILES, KT):
                dve.wait_ge(y_gained, d + 1)
                nc.vector.tensor_tensor(X[:, d, :], X[:, d, :], RS[:, :], ALU.mult).then_inc(yo_done, 1)



def over_pairs(eng, pair):
    pair(0, 0)
    with eng.Fori(0, (NHP - 4) // 2) as t:
        pair(1, t)
        pair(2, t)
    for c in range(NHP - 3, NHP):
        pair(c, 0)


def _constants():
    keys, t = np.arange(PAST), np.arange(PAGE)
    first = np.where(t[:, None] <= keys[None, :], -1.0 / SCALE, 0.0)
    second = np.where(t[:, None] + PAGE <= keys[None, :], -1.0 / SCALE, 0.0)
    new = np.full((PAGE, NS), -1.0 / SCALE)
    b, j = np.arange(NS) // DS, np.arange(NS) % DS
    own = (b[:, None] == b[None, :]) & (j[:, None] <= j[None, :])
    cn = np.concatenate([np.zeros((NS, PAST)), np.where(own, -1.0 / SCALE, 0.0)], axis=1)
    rb, rj = np.arange(2 * NS) // (2 * DS), np.arange(2 * NS) % DS
    seen = (rb[:, None] == b[None, :]) & (j[None, :] <= rj[:, None])
    dm = np.concatenate([np.zeros((2 * NS, PAST)), np.where(seen, 0.0, NEG)], axis=1)
    row = np.arange(P)
    rh = np.arange(2 * NS) // DS % 2
    sel = np.stack([(row[:, None] // NH == rb[None, :]) & (row[:, None] % NH == 2 * hp + rh[None, :])
                    for hp in range(NHP)])
    q = np.arange(P)
    f = np.float32
    return {
        "ones": np.full((P, P), 1.0 / D, f), "ident": np.eye(P, dtype=f),
        "cvec": np.tile(np.array([[EPS, 1.0]], f), (P, 1)),
        "mask": np.where(q[None, :] > q[:, None], NEG, 0.0).astype(f),
        "c0": np.concatenate([first, new], axis=1).astype(f), "c1": np.concatenate([second, new], axis=1).astype(f),
        "cn": cn.astype(f), "dm": dm.astype(f), "sel": sel.astype(f),
    }


def _tiles(w):
    k, m = w.shape
    return np.ascontiguousarray(w.reshape(k // P, P, m // P, P).transpose(2, 1, 0, 3)).reshape(m // P, P, -1)


def _vec(v):
    v = v.reshape(v.shape[:-1] + (-1, P))
    return np.moveaxis(v, -1, 0)


def kernel(x_prompt, x_sample, cache_k, cache_v, cache_logf, state_lru_h, state_lru_conv, state_ffn_conv,
           page_table, norm_a_g, w_a_in, conv_a_w, conv_a_b, w_a_gate, b_a_gate, lru_lambda, w_a_out,
           norm_f_g, w_f_in, conv_f_w, conv_f_b, w_f_out, norm_kv_g, w_kv, b_forget, norm_b_g, w_q, w_o,
           norm_out_g):
    import concourse.bacc as _bacc
    from concourse.bass_utils import run_bass_kernel_spmd as _run
    a = {n: np.asarray(v) for n, v in locals().items() if n not in ("_bacc", "_run")}
    c = np.ascontiguousarray

    x = np.concatenate([a["x_prompt"].reshape(SEQ, D), a["x_sample"].reshape(NS, D)], axis=0)
    w_in = a["w_a_in"][0]
    n_phys = a["cache_k"].shape[0]
    wkv = a["w_kv"]
    gate_up = [_tiles(w) for w in a["w_f_in"]]
    nft = DF // P
    order = [g * nft + FT * s + f for s in range(FSTEPS) for f in range(FT) for g in range(2)]
    arrays = {
        "xT": c(x.T).reshape(KT, P, T),
        "gains": c(np.stack([_vec(g) for g in (a["norm_a_g"][0], a["norm_f_g"][0], a["norm_kv_g"],
                                              a["norm_b_g"][0], a["norm_f_g"][1], a["norm_out_g"])], axis=1)),
        "wa": np.concatenate([_tiles(w_in[:, D:]), _tiles(w_in[:, :D]), _tiles(a["w_a_out"][0])]),
        "wg": c(a["w_a_gate"][0].transpose(1, 0, 2)),
        "apar": c(np.concatenate([_vec(a["conv_a_w"][0]).transpose(0, 2, 1), _vec(a["conv_a_b"][0])[:, :, None],
                                  a["b_a_gate"][0].reshape(KT, 2, P).transpose(2, 0, 1),
                                  _vec(a["lru_lambda"][0])[:, :, None]], axis=2)),
        "conv_state": c(_vec(a["state_lru_conv"][0]).transpose(0, 3, 1, 2)),
        "h0": c(np.pad(_vec(a["state_lru_h"][0]).transpose(0, 2, 1)[..., None], ((0, 0),) * 3 + ((0, DS),))),
        "pages": c(a["page_table"].reshape(1, -1).astype(np.int32)),
        "fpar": c(np.concatenate([a["conv_f_w"], a["conv_f_b"][:, None]], axis=1)
                  .reshape(2, 4, FSTEPS, FT, P).transpose(0, 2, 4, 3, 1)),
        "fst": c(a["state_ffn_conv"].reshape(2, DB, WF - 1, FSTEPS, FT, P).transpose(0, 3, 5, 4, 1, 2)),
        "wfi": np.stack([w[order].reshape(FSTEPS, 2 * FT, P, KT * P) for w in gate_up]),
        "wfo": np.stack([np.stack([_tiles(w[FT * P * s:FT * P * (s + 1)]) for s in range(FSTEPS)])
                         for w in a["w_f_out"]]),
        "wfg": c(wkv[:, 2 * D:].reshape(KT, P, NH).transpose(1, 0, 2)).reshape(P, -1),
        "wqkv": np.stack([_tiles(a["w_q"][0]), _tiles(wkv[:, :D]), _tiles(wkv[:, D:2 * D])], axis=1),
        "wo": _tiles(a["w_o"][0]),
        "bfg": c(a["b_forget"].reshape(NH, 1)),
        "clf": c(a["cache_logf"]),
        "ck": c(a["cache_k"].reshape(n_phys, PAGE, NHP, P).transpose(0, 2, 3, 1)),
        "cv": c(a["cache_v"].reshape(n_phys, PAGE, NHP, P).transpose(0, 2, 1, 3)),
        **_constants(),
    }
    out_shapes = {
        "y": (KT, P, T), "k": (NHP, P, T), "v": (NHP, P, T), "logf": (NH, T), "hlast": (P, KT, 1 + DB),
        "conv_p": (P, KT, WA - 1), "conv_s": (P, KT, DB, WA - 1),
        "ffn_p": (2, FSTEPS, P, FT, WF - 1), "ffn_s": (2, FSTEPS, P, FT, DB, WF - 1),
    }
    nc = _bacc.Bacc("TRN2", target_bir_lowering=False, num_devices=1)
    ins = {n: nc.dram_tensor(f"in_{n}", v.shape, mybir.dt.from_np(v.dtype), kind="ExternalInput").ap()
           for n, v in arrays.items()}
    ins["nf"] = nc.dram_tensor("nf_scratch", (NH, SEQ), F32).ap()
    outs = {n: nc.dram_tensor(f"out_{n}", s, F32, kind="ExternalOutput").ap() for n, s in out_shapes.items()}
    hybrid_step_kernel(nc, ins, outs)
    r = _run(nc, [{f"in_{n}": v for n, v in arrays.items()}], core_ids=[0]).results[0]
    o = {n: np.asarray(r[f"out_{n}"]) for n in out_shapes}

    def rows(y):
        y = y.reshape(D, T)
        return c(y[:, :SEQ].T), c(y[:, SEQ:].T)

    (yp, ys), (kp, ks), (vp, vs) = rows(o["y"]), rows(o["k"]), rows(o["v"])
    heads = (NH, HD)
    h = o["hlast"].transpose(2, 1, 0).reshape(1 + DB, D)
    return (
        yp.reshape(1, SEQ, D), ys.reshape(DB, DS, D),
        kp.reshape(1, SEQ, *heads), vp.reshape(1, SEQ, *heads), c(o["logf"][:, :SEQ].T).reshape(1, SEQ, NH),
        h[None, 0:1], c(o["conv_p"].transpose(2, 1, 0)).reshape(1, 1, WA - 1, D),
        c(o["ffn_p"].transpose(0, 4, 1, 3, 2)).reshape(2, 1, WF - 1, DF),
        ks.reshape(DB, DS, *heads), vs.reshape(DB, DS, *heads), c(o["logf"][:, SEQ:].T).reshape(DB, DS, NH),
        c(h[None, 1:]), c(o["conv_s"].transpose(2, 3, 1, 0)).reshape(1, DB, WA - 1, D),
        c(o["ffn_s"].transpose(0, 4, 5, 1, 3, 2)).reshape(2, DB, WF - 1, DF),
    )
```
